# Optimizing a Trainium2 kernel written in Bass

```python
import jax, jax.numpy as jnp
from jax import lax
import numpy as np

D_MODEL = 1024
BATCH = 1
SEQ = 512
DEPTH = 1
DEC_BATCH = 8
DEC_SEQ = 8
PAST_LEN = 1024
PAGE_SIZE = 128

MIX_DIM = D_MODEL
ATTN_DIM = MIX_DIM // 2
CONV_CH = MIX_DIM - ATTN_DIM
HEAD_DIM = 64
N_HEADS = ATTN_DIM // HEAD_DIM
N_KV_HEADS = 2
GQA_GROUP = N_HEADS // N_KV_HEADS
KV_DIM = N_KV_HEADS * HEAD_DIM
WINDOW = 128
ATTN_BLOCK = WINDOW
CONV_WIDTH = 31
IN_DIM = ATTN_DIM + 2 * KV_DIM + 2 * CONV_CH
SPLITS = [ATTN_DIM, ATTN_DIM + KV_DIM, ATTN_DIM + 2 * KV_DIM, ATTN_DIM + 2 * KV_DIM + CONV_CH]
PEER_HEADS = 8
N_KEYS = 128
N_EXPERTS = N_KEYS * N_KEYS
PEER_TOPK = 16
PEER_QDIM = 256
PEER_HALF = PEER_QDIM // 2
PEER_CHUNK = 128
EPS = 1e-6
NEG = -1e30

kernel_name = "hymba_swa_sink_conformer_peer_step"

def rms_norm(x, g):
    xf = x.astype(jnp.float32)
    y = xf * lax.rsqrt(jnp.mean(xf * xf, axis=-1, keepdims=True) + EPS)
    return (y * g.astype(jnp.float32)).astype(x.dtype)

def layer_norm(x, g, b):
    xf = x.astype(jnp.float32)
    mu = jnp.mean(xf, axis=-1, keepdims=True)
    var = jnp.mean(jnp.square(xf - mu), axis=-1, keepdims=True)
    y = (xf - mu) * lax.rsqrt(var + EPS)
    return (y * g.astype(jnp.float32) + b.astype(jnp.float32)).astype(x.dtype)

def _project(xn, w_in, q_g, k_g):
    lead = xn.shape[:-1]
    z = xn @ w_in
    q, k, v, val, gate = jnp.split(z, SPLITS, axis=-1)
    q = rms_norm(q.reshape(*lead, N_KV_HEADS, GQA_GROUP, HEAD_DIM), q_g)
    k = rms_norm(k.reshape(*lead, N_KV_HEADS, HEAD_DIM), k_g)
    v = v.reshape(*lead, N_KV_HEADS, HEAD_DIM)
    glu = val * jax.nn.sigmoid(gate)
    return q, k, v, glu

def _sink_attend(q, k, v, mask, sinks):
    s = jnp.einsum('...qkgd,...skd->...kgqs', q, k).astype(jnp.float32) * (HEAD_DIM ** -0.5)
    s = jnp.where(mask, s, NEG)
    sink = sinks.astype(jnp.float32).reshape(N_KV_HEADS, GQA_GROUP, 1, 1)
    m = jnp.maximum(jnp.max(s, axis=-1, keepdims=True), sink)
    p = jnp.exp(s - m)
    p = p / (jnp.sum(p, axis=-1, keepdims=True) + jnp.exp(sink - m))
    return jnp.einsum('...kgqs,...skd->...qkgd', p.astype(v.dtype), v)

def _attn_prompt(q, k, v, sinks):
    B, T = q.shape[0], q.shape[1]
    nb = T // ATTN_BLOCK
    qb = q.reshape(B, nb, ATTN_BLOCK, N_KV_HEADS, GQA_GROUP, HEAD_DIM)
    kb = k.reshape(B, nb, ATTN_BLOCK, N_KV_HEADS, HEAD_DIM)
    vb = v.reshape(B, nb, ATTN_BLOCK, N_KV_HEADS, HEAD_DIM)
    prev = lambda t: jnp.concatenate([jnp.zeros_like(t[:, :1]), t[:, :-1]], axis=1)
    kk = jnp.concatenate([prev(kb), kb], axis=2)
    vv = jnp.concatenate([prev(vb), vb], axis=2)
    start = jnp.arange(nb)[:, None, None] * ATTN_BLOCK
    qpos = start + jnp.arange(ATTN_BLOCK)[None, :, None]
    kpos = start + jnp.arange(2 * ATTN_BLOCK)[None, None, :] - ATTN_BLOCK
    mask = (kpos <= qpos) & (kpos > qpos - WINDOW) & (kpos >= 0)
    o = _sink_attend(qb, kk, vv, mask[:, None, None], sinks)
    return o.reshape(B, T, ATTN_DIM)

def _attn_sample(q, k, v, ck, cv, sinks):
    Bd, S = q.shape[0], q.shape[1]
    wb = ck.shape[1]
    kk = jnp.concatenate([ck, k], axis=1)
    vv = jnp.concatenate([cv, v], axis=1)
    qpos = PAST_LEN + jnp.arange(S)[:, None]
    kpos = PAST_LEN - wb + jnp.arange(wb + S)[None, :]
    mask = (kpos <= qpos) & (kpos > qpos - WINDOW)
    o = _sink_attend(q, kk, vv, mask, sinks)
    return o.reshape(Bd, S, ATTN_DIM), kk[:, -wb:], vv[:, -wb:]

def _conv_module(u_padded, w, b, ln_g, ln_b, pw):
    c = lax.conv_general_dilated(u_padded, w[:, None, :], window_strides=(1,), padding='VALID',
                                 dimension_numbers=('NWC', 'WIO', 'NWC'),
                                 feature_group_count=CONV_CH) + b
    return jax.nn.silu(layer_norm(c, ln_g, ln_b)) @ pw

def _merge(a, c, ga, gc, w_out):
    return jnp.concatenate([rms_norm(a, ga), rms_norm(c, gc)], axis=-1) @ w_out

def _peer(xn, wq, keys, u, v):
    lead = xn.shape[:-1]
    xt = xn.reshape(-1, D_MODEL)
    T = xt.shape[0]
    q = (xt @ wq).reshape(T, PEER_HEADS, 2, PEER_HALF).astype(jnp.float32)
    s = jnp.einsum('thpd,hpnd->thpn', q, keys.astype(jnp.float32))
    ts, ti = lax.top_k(s, PEER_TOPK)
    cand_s = (ts[:, :, 0, :, None] + ts[:, :, 1, None, :]).reshape(T, PEER_HEADS, PEER_TOPK * PEER_TOPK)
    cand_i = (ti[:, :, 0, :, None] * N_KEYS + ti[:, :, 1, None, :]).reshape(T, PEER_HEADS, PEER_TOPK * PEER_TOPK)
    best_s, pos = lax.top_k(cand_s, PEER_TOPK)
    idx = jnp.take_along_axis(cand_i, pos, axis=-1)
    gate = jax.nn.softmax(best_s, axis=-1).astype(xn.dtype)
    n_chunks = -(-T // PEER_CHUNK)
    pad = n_chunks * PEER_CHUNK - T
    xc = jnp.pad(xt, ((0, pad), (0, 0))).reshape(n_chunks, PEER_CHUNK, D_MODEL)
    ic = jnp.pad(idx, ((0, pad), (0, 0), (0, 0))).reshape(n_chunks, PEER_CHUNK, PEER_HEADS, PEER_TOPK)
    gc = jnp.pad(gate, ((0, pad), (0, 0), (0, 0))).reshape(n_chunks, PEER_CHUNK, PEER_HEADS, PEER_TOPK)

    def block(args):
        xb, ib, gb = args
        hu = jnp.einsum('chkd,cd->chk', jnp.take(u, ib, axis=0), xb)
        act = jax.nn.gelu(hu, approximate=False) * gb
        return jnp.einsum('chk,chkd->cd', act, jnp.take(v, ib, axis=0))

    out = lax.map(block, (xc, ic, gc)).reshape(-1, D_MODEL)[:T]
    return out.reshape(*lead, D_MODEL)

def setup_inputs(seed: int = 0) -> dict:
    key = jax.random.key(seed)
    ks = jax.random.split(key, 24)
    f32 = jnp.float32
    wbuf = min(WINDOW, PAST_LEN)
    nrm = lambda k, shape, scale: jax.random.normal(k, shape, f32) * scale
    gain = lambda k, shape: 1.0 + 0.02 * jax.random.normal(k, shape, f32)
    return {
        'x_prompt': nrm(ks[0], (BATCH, SEQ, D_MODEL), 1.0),
        'x_sample': nrm(ks[1], (DEC_BATCH, DEC_SEQ, D_MODEL), 1.0),
        'cache_k': nrm(ks[2], (DEPTH, DEC_BATCH, wbuf, N_KV_HEADS, HEAD_DIM), 1.0),
        'cache_v': nrm(ks[3], (DEPTH, DEC_BATCH, wbuf, N_KV_HEADS, HEAD_DIM), 1.0),
        'state_conv': nrm(ks[4], (DEPTH, DEC_BATCH, CONV_WIDTH - 1, CONV_CH), 0.5),
        'norm1_g': gain(ks[5], (DEPTH, D_MODEL)),
        'w_in': nrm(ks[6], (DEPTH, D_MODEL, IN_DIM), D_MODEL ** -0.5),
        'q_norm_g': gain(ks[7], (DEPTH, HEAD_DIM)),
        'k_norm_g': gain(ks[8], (DEPTH, HEAD_DIM)),
        'attn_sinks': nrm(ks[9], (DEPTH, N_HEADS), 0.5),
        'conv_w': nrm(ks[10], (DEPTH, CONV_WIDTH, CONV_CH), CONV_WIDTH ** -0.5),
        'conv_b': nrm(ks[11], (DEPTH, CONV_CH), 0.02),
        'conv_ln_g': gain(ks[12], (DEPTH, CONV_CH)),
        'conv_ln_b': nrm(ks[13], (DEPTH, CONV_CH), 0.02),
        'conv_pw_w': nrm(ks[14], (DEPTH, CONV_CH, CONV_CH), CONV_CH ** -0.5),
        'attn_out_g': gain(ks[15], (DEPTH, ATTN_DIM)),
        'conv_out_g': gain(ks[16], (DEPTH, CONV_CH)),
        'w_out': nrm(ks[17], (DEPTH, MIX_DIM, D_MODEL), MIX_DIM ** -0.5),
        'norm2_g': gain(ks[18], (DEPTH, D_MODEL)),
        'peer_wq': nrm(ks[19], (DEPTH, D_MODEL, PEER_HEADS * PEER_QDIM), D_MODEL ** -0.5),
        'peer_keys': nrm(ks[20], (DEPTH, PEER_HEADS, 2, N_KEYS, PEER_HALF), PEER_HALF ** -0.5),
        'peer_u': nrm(ks[21], (DEPTH, N_EXPERTS, D_MODEL), D_MODEL ** -0.5),
        'peer_v': nrm(ks[22], (DEPTH, N_EXPERTS, D_MODEL), 0.5),
    }

def reference(x_prompt, x_sample, cache_k, cache_v, state_conv, norm1_g, w_in, q_norm_g, k_norm_g,
              attn_sinks, conv_w, conv_b, conv_ln_g, conv_ln_b, conv_pw_w, attn_out_g, conv_out_g,
              w_out, norm2_g, peer_wq, peer_keys, peer_u, peer_v):
    xp, xs = x_prompt, x_sample
    pk, pv, pc, sk, sv, sc = [], [], [], [], [], []
    for l in range(DEPTH):
        xn = rms_norm(xp, norm1_g[l])
        q, k, v, glu = _project(xn, w_in[l], q_norm_g[l], k_norm_g[l])
        a = _attn_prompt(q, k, v, attn_sinks[l])
        zpad = jnp.zeros((xp.shape[0], CONV_WIDTH - 1, CONV_CH), glu.dtype)
        c = _conv_module(jnp.concatenate([zpad, glu], axis=1), conv_w[l], conv_b[l],
                         conv_ln_g[l], conv_ln_b[l], conv_pw_w[l])
        h = xp + _merge(a, c, attn_out_g[l], conv_out_g[l], w_out[l])
        xp = h + _peer(rms_norm(h, norm2_g[l]), peer_wq[l], peer_keys[l], peer_u[l], peer_v[l])
        pk.append(k[:, -WINDOW:])
        pv.append(v[:, -WINDOW:])
        pc.append(glu[:, -(CONV_WIDTH - 1):])
        xn = rms_norm(xs, norm1_g[l])
        q, k, v, glu = _project(xn, w_in[l], q_norm_g[l], k_norm_g[l])
        a, nk, nv = _attn_sample(q, k, v, cache_k[l], cache_v[l], attn_sinks[l])
        u_full = jnp.concatenate([state_conv[l], glu], axis=1)
        c = _conv_module(u_full, conv_w[l], conv_b[l], conv_ln_g[l], conv_ln_b[l], conv_pw_w[l])
        h = xs + _merge(a, c, attn_out_g[l], conv_out_g[l], w_out[l])
        xs = h + _peer(rms_norm(h, norm2_g[l]), peer_wq[l], peer_keys[l], peer_u[l], peer_v[l])
        sk.append(nk)
        sv.append(nv)
        sc.append(u_full[:, -(CONV_WIDTH - 1):])
    return (xp, xs, jnp.stack(pk), jnp.stack(pv), jnp.stack(pc), jnp.stack(sk), jnp.stack(sv), jnp.stack(sc))


_drawn_inputs = setup_inputs


def setup_inputs(seed=0):
    import zlib

    import numpy as np

    out = dict(_drawn_inputs(seed))
    spreads = {}
    factors = {'k_norm_g': 2.861, 'attn_sinks': 3.561, 'conv_ln_b': 2.704}
    for name, (base, spread) in spreads.items():
        noise = np.random.default_rng([zlib.crc32(name.encode()), seed]).standard_normal(out[name].shape)
        drawn = base * np.exp(spread * noise) if base else spread * noise
        out[name] = __import__('jax').numpy.asarray(drawn.astype(out[name].dtype))
    for name, factor in factors.items():
        out[name] = (out[name] * factor).astype(out[name].dtype)
    return out
```

```python
from contextlib import ExitStack

import concourse.bass as bass
from concourse import mybir

ALU = mybir.AluOpType
ACT = mybir.ActivationFunctionType
F32 = mybir.dt.float32
I32 = mybir.dt.int32
U32 = mybir.dt.uint32
AX_X = mybir.AxisListType.X

P = 128
D = 1024
DC = D // P
SEQ = 512
NDB, DS = 8, 8
NS = NDB * DS
T = SEQ + NS
HD = 64
NKV, GQ = 2, 4
NH = NKV * GQ
CC = 4
TAPS = 31
PAD = TAPS - 1
WIN = 128
NEG = -1e30
LOW = -3e38
EPS = 1e-6
PH = 8
NM = 2 * PH
NKEY = 128
TOPK = 16
NPICK = PH * TOPK
NEXP = NKEY * NKEY
RING = 6
GROUP = 16

COLS = {}
_at = 0
for _n, _w in (("g1", DC), ("g2", DC), ("ga", CC), ("gc", CC), ("qg", 1), ("kg", 1), ("cb", CC), ("lg", CC),
               ("lb", CC), ("cw", CC * TAPS), ("sinkp", NH), ("sinks", 1), ("iota", TOPK)):
    COLS[_n] = _at
    _at += _w
NCOL = _at

BLOCKS = ["K", "Q0", "Q1", "Q2", "Q3", "V"]
for _c in range(CC):
    BLOCKS += [f"val{_c}", f"gate{_c}"]
BLOCKS += ["pw0", "pw1"] + [f"wo{_m}" for _m in range(DC)] + [f"wq{_m}" for _m in range(NM)]

TILES = [(0, 128), (128, 128), (256, 128), (384, 128), (512, 64)]


def psum_plan():
    plan = [("ms1", 3), ("K", 0), ("Q0", 1), ("Kn", 3), ("Q1", 2), ("Q0n", 3), ("Q2", 0), ("Q1n", 3), ("Q3", 1),
            ("Q2n", 3), ("V", 2), ("Q3n", 3)]
    for u in range(8):
        plan += [(f"S{u}", 2), (f"glu{u}", u % 2), (f"PT{u}", 3), (f"O{u}", 2)]
    plan += [("SS", 2), ("PTS", 3), ("OS", 2), ("msA", 3), ("mean", 0), ("var", 1)]
    plan += [("pw0", 2), ("pw1", 0), ("pw2", 1), ("pw3", 2), ("msC", 3)]
    plan += [(f"wo{m}", m % 3) for m in range(DC)]
    plan += [("ms2", 3)]
    for m in range(NM):
        plan += [(f"wq{m}", m % 2)]
        if m:
            plan += [(f"sc{m - 1}", 2 + (m - 1) % 2)]
    plan += [(f"sc{NM - 1}", 3)]
    for t in range(len(TILES)):
        plan += [(f"xt{t}", 0), (f"ht{t}", 1)]
    return plan


def hymba_peer(nc, xT_d, wblk_d, cols_d, maskp_d, masks_d, ident_d, ckT_d, cv_d, state_d, keysT_d, u_d, v_d,
               y_d, pk_d, pv_d, pc_d, sk_d, sv_d, sc_d):
    use = {}
    uses = [0] * 4
    for name, pair in psum_plan():
        uses[pair] += 1
        use[name] = (pair, uses[pair])

    with ExitStack() as ctx:
        def sb(name, shape, dt=F32):
            return ctx.enter_context(nc.sbuf_tensor(name, shape, dt))

        def sem(name):
            return ctx.enter_context(nc.semaphore(name))

        ps = [ctx.enter_context(nc.psum_tensor(f"ps{i}", [P, 1024], F32)) for i in range(4)]

        hT = sb("hT", [P, DC, T])
        xn = sb("xn", [P, DC, T])
        mg = sb("mg", [P, DC, T])
        ac = sb("ac", [P, 2 * CC, T])
        AT = ac[:, 0:CC, :]
        cacc = ac[:, CC:2 * CC, :]
        sall = sb("sall", [P, len(TILES), NM, NKEY])
        big = sb("big", [P, GROUP, D])
        bigf = big[:, :, :].rearrange("p a b -> p (a b)")
        off = [0]

        def front(n):
            off[0] += n
            assert off[0] <= GROUP * D
            return bigf[:, off[0] - n:off[0]]

        wring = front(RING * 1024).rearrange("p (a b) -> p a b", a=RING)
        qT = front(CC * T).rearrange("p (a b) -> p a b", a=CC)
        kT = front(T)
        vtok = front(5 * P).rearrange("p (a b) -> p a b", a=5)
        sq = front(2 * T).rearrange("p (a b) -> p a b", a=2)
        Pb = front(1024)
        PTb = front(1024)
        q2T = front(2 * T).rearrange("p (a b) -> p a b", a=2)
        maskp = front(2 * WIN)
        ptmp = front(T)
        qS = front(NDB * GQ * DS)
        masks = front(4 * (WIN + NS)).rearrange("p (a b) -> p a b", a=4)
        ckT = sb("ckT", [P, NDB, WIN])
        cv = sb("cv", [P, NDB, P])
        acc = ckT[:, :, :].rearrange("p b c -> p (b c)")
        rs = sb("rs", [P, T])
        keysT = sb("keysT", [P, NM, NKEY])
        gpad = sall[:, 0:2, :, :].rearrange("p a m n -> p (a m n)")[:, 0:CC * (PAD + SEQ)].rearrange(
            "p (c t) -> p c t", c=CC)
        spad = sall[:, 2:3, :, :].rearrange("p a m n -> p (a m n)")[:, 0:CC * NDB * (PAD + DS)].rearrange(
            "p (c b t) -> p c b t", c=CC, b=NDB)
        cols = sb("cols_sb", [P, NCOL])
        ident = sb("ident_sb", [P, P])
        on1024 = sb("on1024", [P, P])
        on512 = sb("on512", [P, P])
        onblk = sb("onblk", [P, P])
        epst = sb("epst", [P, 1])
        st = sb("st", [P, 8, 8])
        idxf = sb("idxf", [P, NPICK])
        idx = sb("idx", [P, len(TILES), NPICK], I32)
        gate = sb("gate", [P, len(TILES), NPICK])
        hu = sb("hu", [P, NPICK])
        hu16 = sb("hu16", [P, GROUP])
        a16 = sb("a16", [P, GROUP])
        idx16 = sb("idx16", [P, GROUP], I32)
        mgf = mg[:, :, :].rearrange("p a b -> p (a b)")
        tsv = mgf[:, 1024:1280].rearrange("p (m k) -> p m k", m=NM)
        tsi = mgf[:, 1280:1536].bitcast(U32).rearrange("p (m k) -> p m k", m=NM)
        bv = mgf[:, 1536:1664].rearrange("p (h k) -> p h k", h=PH)
        bi = mgf[:, 1664:1792].bitcast(U32).rearrange("p (h k) -> p h k", h=PH)
        bt = mgf[:, 1792:2304].rearrange("p (a h k) -> p a h k", a=4, h=PH)
        bu = mgf[:, 2304:2560].bitcast(U32).rearrange("p (a h k) -> p a h k", a=2, h=PH)
        scr = ac[:, :, :].rearrange("p a b -> p (a b)")
        cand = scr[:, 0:2048].rearrange("p (h k) -> p h k", h=PH)
        oneh = scr[:, 2048:4096].rearrange("p (h k a) -> p h k a", h=PH, a=TOPK)
        xtok = mg[:, :, :].rearrange("p a b -> p (a b)")[:, 0:4096].rearrange("p (t d) -> p t d", t=4)

        def col(name, i=0, n=1):
            return cols[:, COLS[name] + i:COLS[name] + i + n]

        R = [sem(f"psum_ready{i}") for i in range(4)]
        F = [sem(f"psum_free{i}") for i in range(4)]
        w_in = [sem(f"w_landed{i}") for i in range(RING)]
        w_used = sem("w_used")
        s_x = sem("x_landed")
        s_ct = sem("consts_landed")
        s_cache = sem("caches_landed")
        s_ones = sem("ones_set")
        s_sq1 = sem("sq1_ready")
        s_rt = sem("root_ready")
        s_rs = sem("rstd_ready")
        s_xn = sem("xn_ready")
        s_sqk = sem("sq_qk_ready")
        s_qk = sem("qk_ready")
        s_v = sem("v_ready")
        s_sig = sem("sigmoid_ready")
        s_glu = sem("glu_ready")
        s_stpad = sem("state_landed")
        s_pz = sem("pad_zeroed")
        s_conv_p = sem("conv_by_pool")
        s_conv_d = sem("conv_by_dve")
        s_nm = sem("negmax_ready")
        s_ex = sem("exp_ready")
        s_p = sem("probs_ready")
        s_pt = sem("probsT_ready")
        s_at = sem("attn_out_ready")
        s_sqa = sem("sqA_ready")
        s_dm = sem("centred_ready")
        s_sqc = sem("sq_centred_ready")
        s_ln = sem("ln_ready")
        s_sw = sem("swish_ready")
        s_craw = sem("conv_raw_ready")
        s_sqcr = sem("sq_conv_raw_ready")
        s_mg = sem("merged_ready")
        s_h = sem("h_ready")
        s_sqh = sem("sqh_ready")
        s_xn2 = sem("xn2_ready")
        s_q2 = sem("q2_ready")
        s_sc = sem("scores_ready")
        s_top = sem("topk_ready")
        s_xt = sem("xtok_ready")
        s_ht = sem("htok_ready")
        g_in = [sem(f"row_landed{i}") for i in range(GROUP)]
        g_used = sem("row_used")
        s_ix = sem("idx16_ready")
        s_ixw = sem("idx16_waited")
        s_huc = sem("hu_copied")
        s_hu = sem("hu_tile_done")
        s_gel = sem("gelu_ready")
        s_act = sem("act_ready")
        s_ad = sem("act_chain")
        s_dd = sem("dve_chain")
        s_pd = sem("pool_chain")
        s_y = sem("acc_done")
        s_out = sem("y_stored")
        s_o2 = sem("small_outputs_stored")

        def mid(ap):
            return ap.rearrange("p (b s) -> p b s", b=NDB)

        block = ctx.enter_context(nc.Block())

        @block.sync
        def _(sp):
            def small_outputs():
                sp.wait_ge(s_qk, 5)
                sp.wait_ge(s_v, 2)
                sp.wait_ge(s_glu, 2 * CC)
                sp.wait_ge(s_cache, 48)
                sp.dma_start(pk_d, kT[:, SEQ - WIN:SEQ]).then_inc(s_o2, 16)
                sp.dma_start(pv_d, vtok[:, 3, :]).then_inc(s_o2, 16)
                sp.dma_start(pc_d, gpad[:, :, SEQ:SEQ + PAD]).then_inc(s_o2, 16)
                sp.dma_start(sk_d[:, :, 0:WIN - DS], ckT[:, :, DS:WIN]).then_inc(s_o2, 16)
                sp.dma_start(sk_d[:, :, WIN - DS:WIN], mid(kT[:, SEQ:T])).then_inc(s_o2, 16)
                sp.dma_start(sv_d[0:WIN - DS, :, :], cv[DS:WIN, :, :]).then_inc(s_o2, 16)
                for b in range(NDB):
                    sp.dma_start(sv_d[WIN - DS:WIN, b, :], vtok[b * DS:(b + 1) * DS, 4, :]).then_inc(s_o2, 16)
                sp.dma_start(sc_d, spad[:, :, :, DS:DS + PAD]).then_inc(s_o2, 16)

            sp.dma_start(hT[:, :, :], xT_d).then_inc(s_x, 16)
            for n in range(len(BLOCKS)):
                if n == 1:
                    sp.dma_start(cols[:, :], cols_d).then_inc(s_ct, 16)
                    sp.dma_start(maskp[:, :], maskp_d).then_inc(s_ct, 16)
                    sp.dma_start(masks[:, :, :], masks_d).then_inc(s_ct, 16)
                    sp.dma_start(ident[:, :], ident_d).then_inc(s_ct, 16)
                if n == 3:
                    sp.dma_start(spad[:, :, :, 0:PAD], state_d).then_inc(s_stpad, 16)
                    sp.dma_start(ckT[:, :, :], ckT_d).then_inc(s_cache, 16)
                    sp.dma_start(cv[:, :, :], cv_d).then_inc(s_cache, 16)
                    sp.dma_start(keysT[:, :, :], keysT_d).then_inc(s_cache, 16)
                if BLOCKS[n] == "wo0":
                    small_outputs()
                if n >= RING:
                    sp.wait_ge(w_used, n - RING + 1)
                sp.dma_start(wring[:, n % RING, :], wblk_d[n]).then_inc(w_in[n % RING], 16)
            for t, (t0, n) in enumerate(TILES):
                sp.wait_ge(s_y, t + 1)
                sp.dma_start(y_d[t0:t0 + n, :], acc[0:n, :]).then_inc(s_out, 16)
            sp.wait_ge(s_out, 16 * len(TILES))
            sp.wait_ge(s_o2, 16 * 15)

        @block.tensor
        def _(pe):
            nblk = [0]

            def take(name):
                pair, n = use[name]
                if n > 1:
                    pe.wait_ge(F[pair], n - 1)
                return ps[pair], R[pair]

            def gemm(name, rhs, kc=DC, cut=0, last=True):
                out, ready = take(name)
                n = nblk[0]
                if cut == 0:
                    pe.wait_ge(w_in[n % RING], 16 * (n // RING + 1))
                for k in range(kc):
                    w = wring[:, n % RING, (cut + k) * P:(cut + k + 1) * P]
                    nc.tensor.matmul(out[:, 0:SEQ], w, rhs[:, k, 0:SEQ], start=(k == 0), stop=(k == kc - 1))
                    mm = nc.tensor.matmul(out[:, SEQ:T], w, rhs[:, k, SEQ:T], start=(k == 0), stop=(k == kc - 1))
                mm.then_inc(ready, 1)
                if last:
                    nblk[0] += 1

            def free_block():
                pe.wait_ge(R[last_pair[0]], last_use[0])
                pe.sem_inc(w_used, 1)

            last_pair, last_use = [0], [0]

            def gemm_block(name, rhs, kc=DC, cut=0, last=True):
                gemm(name, rhs, kc, cut, last)
                last_pair[0], last_use[0] = use[name]

            def means(name, ones, src, n):
                out, ready = take(name)
                for k in range(n):
                    nc.tensor.matmul(out[:, 0:SEQ], ones[:, :], src(k)[:, 0:SEQ], start=(k == 0), stop=(k == n - 1))
                    mm = nc.tensor.matmul(out[:, SEQ:T], ones[:, :], src(k)[:, SEQ:T], start=(k == 0), stop=(k == n - 1))
                mm.then_inc(ready, 1)

            pe.wait_ge(s_ones, 5)
            pe.wait_ge(s_sq1, DC)
            means("ms1", on1024, lambda k: mg[:, k, :], DC)
            pe.wait_ge(s_xn, DC)

            def norm_qk(i):
                pe.wait_ge(s_sqk, i + 1)
                means(["Kn", "Q0n", "Q1n", "Q2n", "Q3n"][i], onblk, lambda k: sq[:, i % 2, :], 1)

            gemm_block("K", xn)
            free_block()
            gemm_block("Q0", xn)
            free_block()
            norm_qk(0)
            for j in range(1, 4):
                gemm_block(f"Q{j}", xn)
                free_block()
                norm_qk(j)
            out, ready = take("V")
            n = nblk[0]
            pe.wait_ge(w_in[n % RING], 16 * (n // RING + 1))
            for t, (t0, w) in enumerate(TILES):
                for k in range(DC):
                    mm = nc.tensor.matmul(out[0:w, t * P:(t + 1) * P], xn[:, k, t0:t0 + w],
                                          wring[:, n % RING, k * P:(k + 1) * P], start=(k == 0), stop=(k == DC - 1))
            mm.then_inc(ready, 1)
            nblk[0] += 1
            last_pair[0], last_use[0] = use["V"]
            free_block()
            norm_qk(4)
            pe.wait_ge(s_qk, 6)
            pe.wait_ge(s_v, 2)
            pe.wait_ge(s_ct, 64)
            for u in range(8):
                t, g = u // 2, u % 2
                rows = slice(g * HD, (g + 1) * HD)
                k0 = 0 if t else WIN
                out, ready = take(f"S{u}")
                for j in range(GQ):
                    mm = nc.tensor.matmul(out[:, j * 256 + k0:(j + 1) * 256], qT[rows, j, t * P:(t + 1) * P],
                                          kT[rows, t * P - P + k0:(t + 1) * P], start=True, stop=True)
                mm.then_inc(ready, 1)
                gemm_block(f"glu{u}", xn)
                free_block()
                pe.wait_ge(s_p, u + 1)
                out, ready = take(f"PT{u}")
                for j in range(GQ):
                    for kb in range(k0 // WIN, 2):
                        mm = nc.tensor.transpose(out[:, (j * 2 + kb) * P:(j * 2 + kb + 1) * P],
                                                 Pb[:, (j * 2 + kb) * P:(j * 2 + kb + 1) * P], ident[:, :])
                mm.then_inc(ready, 1)
                pe.wait_ge(s_pt, u + 1)
                out, ready = take(f"O{u}")
                for j in range(GQ):
                    for kb in range(k0 // WIN, 2):
                        mm = nc.tensor.matmul(out[rows, j * P:(j + 1) * P], vtok[:, t - 1 + kb, g * HD:(g + 1) * HD],
                                              PTb[:, (j * 2 + kb) * P:(j * 2 + kb + 1) * P],
                                              start=(kb == k0 // WIN), stop=(kb == 1))
                mm.then_inc(ready, 1)
            pe.wait_ge(s_cache, 48)
            out, ready = take("SS")
            for b in range(NDB):
                for g in range(NKV):
                    grp, slot = b // 2, (b % 2) * 2 + g
                    rows = slice(g * HD, (g + 1) * HD)
                    o = out[slot * 32:slot * 32 + 32, (grp // 2) * 512 + (grp % 2) * 192:]
                    q = qS[rows, b * 32:(b + 1) * 32]
                    nc.tensor.matmul(o[:, 0:WIN], q, ckT[rows, b, :], start=True, stop=True)
                    mm = nc.tensor.matmul(o[:, WIN:WIN + NS], q, kT[rows, SEQ:T], start=True, stop=True)
            mm.then_inc(ready, 1)
            pe.wait_ge(s_p, 9)
            out, ready = take("PTS")
            for grp in range(4):
                nc.tensor.transpose(out[:, grp * P:(grp + 1) * P], Pb[:, grp * 192:grp * 192 + WIN], ident[:, :])
                mm = nc.tensor.transpose(out[0:NS, 512 + grp * P:512 + (grp + 1) * P],
                                         Pb[:, grp * 192 + WIN:(grp + 1) * 192], ident[:, :])
            mm.then_inc(ready, 1)
            pe.wait_ge(s_pt, 9)
            out, ready = take("OS")
            for b in range(NDB):
                for g in range(NKV):
                    grp, slot = b // 2, (b % 2) * 2 + g
                    rows = slice(g * HD, (g + 1) * HD)
                    c = grp * P + slot * 32
                    nc.tensor.matmul(out[rows, b * 32:b * 32 + 32], cv[:, b, rows], PTb[:, c:c + 32],
                                     start=True, stop=False)
                    mm = nc.tensor.matmul(out[rows, b * 32:b * 32 + 32], vtok[0:NS, 4, rows],
                                          PTb[0:NS, 512 + c:512 + c + 32], start=False, stop=True)
            mm.then_inc(ready, 1)
            pe.wait_ge(s_sqa, CC)
            means("msA", on512, lambda k: mg[:, k, :], CC)
            pe.wait_ge(s_conv_p, 1)
            pe.wait_ge(s_conv_d, 3)
            means("mean", on512, lambda k: cacc[:, k, :], CC)
            pe.wait_ge(s_sqc, CC)
            means("var", on512, lambda k: mg[:, CC + k, :], CC)
            pe.wait_ge(s_sw, CC)
            for m in range(CC):
                gemm_block(f"pw{m}", cacc, kc=CC, cut=(m % 2) * CC, last=(m % 2 == 1))
                if m % 2 == 1:
                    free_block()
            pe.wait_ge(s_sqcr, CC)
            means("msC", on512, lambda k: mg[:, CC + k, :], CC)
            pe.wait_ge(s_mg, 2 * CC)
            for m in range(DC):
                gemm_block(f"wo{m}", mg)
                free_block()
            pe.wait_ge(s_sqh, DC)
            means("ms2", on1024, lambda k: xn[:, k, :], DC)
            pe.wait_ge(s_xn2, DC)

            def scores(m):
                pe.wait_ge(s_q2, m + 1)
                out, ready = take(f"sc{m}")
                for t, (t0, w) in enumerate(TILES):
                    mm = nc.tensor.matmul(out[0:w, t * P:(t + 1) * P], q2T[:, m % 2, t0:t0 + w], keysT[:, m, :],
                                          start=True, stop=True)
                mm.then_inc(ready, 1)

            for m in range(NM):
                gemm_block(f"wq{m}", xn)
                free_block()
                if m:
                    scores(m - 1)
            scores(NM - 1)
            for t, (t0, w) in enumerate(TILES):
                for name, src in ((f"xt{t}", xn), (f"ht{t}", hT)):
                    out, ready = take(name)
                    for c in range(DC):
                        mm = nc.tensor.transpose(out[0:w, c * P:(c + 1) * P], src[:, c, t0:t0 + w], ident[:, :])
                    mm.then_inc(ready, 1)

        @block.scalar
        def _(act):
            chain = [0]

            def link(ins):
                chain[0] += 1
                ins.then_inc(s_ad, 1)
                act.wait_ge(s_ad, chain[0])

            def ready(name):
                pair, n = use[name]
                act.wait_ge(R[pair], n)
                return ps[pair]

            roots = [0]

            def root(name):
                p = ready(name)
                nc.scalar.activation(rs[:, :], p[:, 0:T], ACT.Sqrt, bias=epst[:, :]).then_inc(s_rt, 1)
                roots[0] += 1

            act.wait_ge(s_x, 16)
            for c in range(DC):
                nc.scalar.activation(mg[:, c, :], hT[:, c, :], ACT.Square).then_inc(s_sq1, 1)
            act.wait_ge(s_ones, 5)
            root("ms1")
            for i, name in enumerate(["K", "Q0", "Q1", "Q2", "Q3"]):
                p = ready(name)
                if i >= 2:
                    act.wait_ge(R[3], use[["Kn", "Q0n", "Q1n", "Q2n", "Q3n"][i - 2]][1])
                nc.scalar.activation(sq[:, i % 2, :], p[:, 0:T], ACT.Square).then_inc(s_sqk, 1)
                act.wait_ge(s_qk if i else s_xn, i or DC)
                root(["Kn", "Q0n", "Q1n", "Q2n", "Q3n"][i])
            p = ready("V")
            nc.scalar.activation(vtok[:, 0:4, :], p[:, 0:512].rearrange("p (a b) -> p a b", a=4), ACT.Copy).then_inc(s_v, 1)
            nc.scalar.activation(vtok[0:NS, 4, :], p[0:NS, 512:640], ACT.Copy).then_inc(s_v, 1)
            act.wait_ge(s_v, 2)
            act.sem_inc(F[use["V"][0]], 1)

            def exps(u, n, view, sink, o):
                act.wait_ge(s_nm, u + 1)
                for j in range(n):
                    nc.scalar.activation(view(j), view(j), ACT.Exp, bias=st[:, 1, o + j:o + j + 1],
                                         accum_out=st[:, 2, o + j:o + j + 1])
                nc.scalar.activation(st[:, 3, o:o + n], st[:, 3, o:o + n], ACT.Exp).then_inc(s_ex, 1)

            for u in range(8):
                k0 = 0 if u // 2 else WIN
                exps(u, GQ, lambda j: Pb[:, j * 256 + k0:(j + 1) * 256], None, 0)
                if u % 2 == 1:
                    c = u // 2
                    p = ready(f"glu{u}")
                    nc.scalar.activation(q2T[:, c % 2, :], p[:, 0:T], ACT.Sigmoid).then_inc(s_sig, 1)
                    act.wait_ge(s_sig, c + 1)
                    act.sem_inc(F[use[f"glu{u}"][0]], 1)
                p = ready(f"PT{u}")
                if k0:
                    v = p[:, :].rearrange("p (j k q) -> p j k q", j=GQ, k=2)[:, :, 1, :]
                    o = PTb.rearrange("p (j k q) -> p j k q", j=GQ, k=2)[:, :, 1, :]
                else:
                    v, o = p[:, :], PTb
                if u:
                    act.wait_ge(R[2], use[f"O{u - 1}"][1])
                nc.scalar.activation(o, v, ACT.Copy).then_inc(s_pt, 1)
                act.wait_ge(s_pt, u + 1)
                act.sem_inc(F[3], 1)
            exps(8, 4, lambda j: Pb[:, j * 192:(j + 1) * 192], None, 0)
            p = ready("PTS")
            act.wait_ge(R[2], use["O7"][1])
            link(nc.scalar.activation(PTb[:, 0:512], p[:, 0:512], ACT.Copy))
            nc.scalar.activation(PTb[0:NS, 512:1024], p[0:NS, 512:1024], ACT.Copy).then_inc(s_pt, 1)
            act.wait_ge(s_pt, 9)
            act.sem_inc(F[3], 1)
            act.wait_ge(s_at, 9)
            for c in range(CC):
                nc.scalar.activation(mg[:, c, :], AT[:, c, :], ACT.Square).then_inc(s_sqa, 1)
            root("msA")
            act.wait_ge(s_mg, CC)
            for c in range(CC):
                act.wait_ge(s_dm, c + 1)
                nc.scalar.activation(mg[:, CC + c, :], cacc[:, c, :], ACT.Square).then_inc(s_sqc, 1)
            root("var")
            for c in range(CC):
                act.wait_ge(s_ln, c + 1)
                nc.scalar.activation(cacc[:, c, :], cacc[:, c, :], ACT.Silu, bias=col("lb", c),
                                     scale=col("lg", c)).then_inc(s_sw, 1)
            for c in range(CC):
                p = ready(f"pw{c}")
                nc.scalar.activation(AT[:, c, :], p[:, 0:T], ACT.Copy).then_inc(s_craw, 1)
                nc.scalar.activation(mg[:, CC + c, :], p[:, 0:T], ACT.Square).then_inc(s_sqcr, 1)
                act.wait_ge(s_sqcr, c + 1)
                act.sem_inc(F[use[f"pw{c}"][0]], 1)
            root("msC")
            for m in range(DC):
                act.wait_ge(s_h, m + 1)
                nc.scalar.activation(xn[:, m, :], hT[:, m, :], ACT.Square).then_inc(s_sqh, 1)
            act.wait_ge(s_mg, 2 * CC)
            root("ms2")

            def score_out(m):
                p = ready(f"sc{m}")
                nc.scalar.activation(sall[:, 0:4, m, :], p[:, 0:512].rearrange("p (a b) -> p a b", a=4), ACT.Copy)
                nc.scalar.activation(sall[0:NS, 4, m, :], p[0:NS, 512:640], ACT.Copy).then_inc(s_sc, 1)
                act.wait_ge(s_sc, m + 1)
                act.sem_inc(F[use[f"sc{m}"][0]], 1)

            act.wait_ge(s_o2, 16 * 15)
            for m in range(NM):
                p = ready(f"wq{m}")
                if m >= 2:
                    pair, n = use[f"sc{m - 2}"]
                    act.wait_ge(R[pair], n)
                nc.scalar.activation(q2T[:, m % 2, :], p[:, 0:T], ACT.Copy).then_inc(s_q2, 1)
                act.wait_ge(s_q2, m + 1)
                act.sem_inc(F[use[f"wq{m}"][0]], 1)
                if m:
                    score_out(m - 1)
            score_out(NM - 1)
            for t, (t0, w) in enumerate(TILES):
                act.wait_ge(s_top, 2 * t + 1)
                nc.scalar.activation(gate[0:w, t, :], gate[0:w, t, :], ACT.Exp).then_inc(s_ex, 1)
            for t, (t0, w) in enumerate(TILES):
                if t:
                    act.wait_ge(s_y, t)
                    act.wait_ge(s_out, 16 * t)
                p = ready(f"xt{t}")
                link(nc.scalar.activation(xtok[0:w, 0, :], p[0:w, :], ACT.Copy))
                act.sem_inc(F[0], 1)
                p = ready(f"ht{t}")
                nc.scalar.activation(acc[0:w, :], p[0:w, :], ACT.Copy).then_inc(s_xt, 1)
                act.wait_ge(s_xt, t + 1)
                act.sem_inc(F[1], 1)
                act.wait_ge(s_hu, t + 1)
                nc.scalar.activation(hu[0:w, :], hu[0:w, :], ACT.Gelu).then_inc(s_gel, 1)

        @block.gpsimd
        def _(pool):
            chain = [0]

            def link(ins):
                chain[0] += 1
                ins.then_inc(s_pd, 1)
                pool.wait_ge(s_pd, chain[0])

            link(nc.gpsimd.memset(onblk[:, :], 0.0))
            for n, (part, value) in enumerate(((on1024[:, :], 1.0 / D), (on512[:, :], 1.0 / (CC * P)),
                                               (onblk[0:HD, 0:HD], 1.0 / HD), (onblk[HD:P, HD:P], 1.0 / HD),
                                               (epst[:, :], EPS))):
                nc.gpsimd.memset(part, value).then_inc(s_ones, 1)
                pool.wait_ge(s_ones, n + 1)
            nc.gpsimd.memset(gpad[:, :, 0:PAD], 0.0).then_inc(s_pz, 1)
            conv_chunks(pool, nc.gpsimd, (0,), gpad, spad, cacc, col, s_glu, s_pz, s_stpad, s_conv_p, link, mid, ptmp)
            pool.sem_inc(g_used, 1)
            turn = 0
            for t, (t0, w) in enumerate(TILES):
                pool.wait_ge(s_top, 2 * t + 2)
                if t == 0:
                    pool.wait_ge(s_sc, NM)
                    pool.wait_ge(s_o2, 16 * 15)
                for half, table in enumerate((u_d, v_d)):
                    with pool.Fori(0, NPICK // GROUP) as i:
                        pool.wait_ge(g_used, (turn + i) * GROUP + 1)
                        pool.sem_inc(s_ixw, 1)
                        pool.tensor_copy(idx16[0:w, :], idx[0:w, t, bass.ds(i * GROUP, GROUP)]).then_inc(s_ix, 1)
                        pool.wait_ge(s_ix, turn + i + 1)
                        pool.sem_inc(s_ixw, 1)
                        for k in range(GROUP):
                            pool.indirect_dma_start(big[0:w, k, :], None, table,
                                                    bass.IndirectOffsetOnAxis(idx16[0:w, k:k + 1], 0)).then_inc(g_in[k], 16)
                    turn += NPICK // GROUP

        @block.vector
        def _(dve):
            chain = [0]

            def link(ins):
                chain[0] += 1
                ins.then_inc(s_dd, 1)
                dve.wait_ge(s_dd, chain[0])

            def ready(name):
                pair, n = use[name]
                dve.wait_ge(R[pair], n)
                return ps[pair]

            nrt = [0]

            def rstd(name):
                nrt[0] += 1
                dve.wait_ge(s_rt, nrt[0])
                nc.vector.reciprocal(rs[:, :], rs[:, :]).then_inc(F[use[name][0]], 1)
                pair, n = use[name]
                dve.wait_ge(F[pair], n)

            dve.wait_ge(s_ct, 64)
            rstd("ms1")
            for c in range(DC):
                nc.vector.scalar_tensor_tensor(out=xn[:, c, :], in0=hT[:, c, :], scalar=col("g1", c), in1=rs[:, :],
                                               op0=ALU.mult, op1=ALU.mult).then_inc(s_xn, 1)
            dve.wait_ge(s_xn, DC)
            for i, (raw, nm) in enumerate([("K", "Kn"), ("Q0", "Q0n"), ("Q1", "Q1n"), ("Q2", "Q2n"), ("Q3", "Q3n")]):
                rstd(nm)
                dst = kT if i == 0 else qT[:, i - 1, :]
                nc.vector.scalar_tensor_tensor(out=dst, in0=ps[use[raw][0]][:, 0:T],
                                               scalar=col("kg") if i == 0 else col("qg"), in1=rs[:, :],
                                               op0=ALU.mult, op1=ALU.mult).then_inc(s_qk, 1)
                dve.wait_ge(s_qk, i + 1)
                dve.sem_inc(F[use[raw][0]], 1)

            nc.vector.tensor_copy(qS.rearrange("p (b j s) -> p b j s", b=NDB, j=GQ),
                                  qT[:, :, SEQ:T].rearrange("p j (b s) -> p b j s", b=NDB)).then_inc(s_qk, 1)

            def softmax_max(u, S, n, sink):
                link(nc.vector.tensor_reduce(st[:, 0, 0:n], S, AX_X, ALU.max))
                link(nc.vector.tensor_tensor(st[:, 0, 0:n], st[:, 0, 0:n], sink, ALU.max))
                link(nc.vector.tensor_tensor(st[:, 3, 0:n], sink, st[:, 0, 0:n], ALU.subtract))
                nc.vector.tensor_scalar(st[:, 1, 0:n], st[:, 0, 0:n], -1.0, None, ALU.mult).then_inc(s_nm, 1)

            def softmax_div(u, S, n, w):
                dve.wait_ge(s_ex, u + 1)
                link(nc.vector.tensor_tensor(st[:, 4, 0:n], st[:, 2, 0:n], st[:, 3, 0:n], ALU.add))
                link(nc.vector.reciprocal(st[:, 5, 0:n], st[:, 4, 0:n]))
                nc.vector.tensor_tensor(S, S, st[:, 5, 0:n].unsqueeze(2).broadcast_to([P, n, w]),
                                        ALU.mult).then_inc(s_p, 1)

            for u in range(8):
                t, g = u // 2, u % 2
                k0 = 0 if t else WIN
                p = ready(f"S{u}")
                S = Pb.rearrange("p (j k) -> p j k", j=GQ)[:, :, k0:]
                if u:
                    dve.wait_ge(R[3], use[f"PT{u - 1}"][1])
                nc.vector.scalar_tensor_tensor(
                    out=S, in0=p[:, :].rearrange("p (j k) -> p j k", j=GQ)[:, :, k0:], scalar=HD ** -0.5,
                    in1=maskp[:, k0:].unsqueeze(1).broadcast_to([P, GQ, 2 * WIN - k0]), op0=ALU.mult,
                    op1=ALU.add).then_inc(F[2], 1)
                dve.wait_ge(F[2], use[f"S{u}"][1])
                softmax_max(u, S, GQ, col("sinkp", g * GQ, GQ))
                if u % 2 == 1:
                    c = u // 2
                    v = ready(f"glu{u - 1}")
                    dve.wait_ge(s_sig, c + 1)
                    if c == 0:
                        dve.wait_ge(s_stpad, 16)
                    nc.vector.tensor_tensor(gpad[:, c, PAD:], v[:, 0:SEQ], q2T[:, c % 2, 0:SEQ], ALU.mult).then_inc(s_glu, 1)
                    nc.vector.tensor_tensor(spad[:, c, :, PAD:], mid(v[:, SEQ:T]), mid(q2T[:, c % 2, SEQ:T]),
                                            ALU.mult).then_inc(s_glu, 1)
                    dve.wait_ge(s_glu, 2 * c + 2)
                    dve.sem_inc(F[use[f"glu{u - 1}"][0]], 1)
                softmax_div(u, S, GQ, 2 * WIN - k0)
                p = ready(f"O{u}")
                rows = slice(g * HD, (g + 1) * HD)
                nc.vector.tensor_copy(AT[rows, :, t * P:(t + 1) * P],
                                      p[rows, 0:512].rearrange("p (j q) -> p j q", j=GQ)).then_inc(s_at, 1)
                dve.wait_ge(s_at, u + 1)
                dve.sem_inc(F[2], 1)
            p = ready("SS")
            S = Pb[:, 0:768].rearrange("p (j k) -> p j k", j=4)
            for half in range(2):
                ins = nc.vector.scalar_tensor_tensor(
                    out=S[:, 2 * half:2 * half + 2, :],
                    in0=p[:, half * 512:half * 512 + 384].rearrange("p (j k) -> p j k", j=2), scalar=HD ** -0.5,
                    in1=masks[:, 2 * half:2 * half + 2, :], op0=ALU.mult, op1=ALU.add)
            ins.then_inc(F[2], 1)
            dve.wait_ge(F[2], use["SS"][1])
            softmax_max(8, S, 4, col("sinks").broadcast_to([P, 4]))
            softmax_div(8, S, 4, WIN + NS)
            p = ready("OS")
            nc.vector.tensor_copy(AT[:, :, SEQ:T].rearrange("p j (b s) -> p b j s", b=NDB),
                                  p[:, 0:256].rearrange("p (b j s) -> p b j s", b=NDB, j=GQ)).then_inc(s_at, 1)
            dve.wait_ge(s_at, 9)
            dve.sem_inc(F[2], 1)
            conv_chunks(dve, nc.vector, (1, 2, 3), gpad, spad, cacc, col, s_glu, s_pz, s_stpad, s_conv_d, link, mid)

            def merged(c, src, gain, rowc):
                nc.vector.scalar_tensor_tensor(out=mg[:, c, :], in0=src, scalar=col(gain, rowc), in1=rs[:, :],
                                               op0=ALU.mult, op1=ALU.mult).then_inc(s_mg, 1)

            rstd("msA")
            for c in range(CC):
                merged(c, AT[:, c, :], "ga", c)
            dve.wait_ge(s_mg, CC)
            p = ready("mean")
            for c in range(CC):
                nc.vector.tensor_tensor(cacc[:, c, :], cacc[:, c, :], p[:, 0:T], ALU.subtract).then_inc(s_dm, 1)
            dve.wait_ge(s_dm, CC)
            dve.sem_inc(F[0], 1)
            rstd("var")
            for c in range(CC):
                dve.wait_ge(s_sqc, c + 1)
                nc.vector.tensor_tensor(cacc[:, c, :], cacc[:, c, :], rs[:, :], ALU.mult).then_inc(s_ln, 1)
            dve.wait_ge(s_ln, CC)
            rstd("msC")
            for c in range(CC):
                dve.wait_ge(s_craw, c + 1)
                merged(CC + c, AT[:, c, :], "gc", c)
            for m in range(DC):
                p = ready(f"wo{m}")
                nc.vector.tensor_tensor(hT[:, m, :], hT[:, m, :], p[:, 0:T], ALU.add).then_inc(s_h, 1)
                dve.wait_ge(s_h, m + 1)
                dve.sem_inc(F[use[f"wo{m}"][0]], 1)
            rstd("ms2")
            for c in range(DC):
                nc.vector.scalar_tensor_tensor(out=xn[:, c, :], in0=hT[:, c, :], scalar=col("g2", c), in1=rs[:, :],
                                               op0=ALU.mult, op1=ALU.mult).then_inc(s_xn2, 1)
            dve.wait_ge(s_sc, NM)
            dve.wait_ge(s_sw, CC)
            for t, (t0, w) in enumerate(TILES):
                for m in range(NM):
                    s = sall[0:w, t, m, :]
                    link(nc.vector.max(tsv[0:w, m, 0:8], s))
                    link(nc.vector.max_index(tsi[0:w, m, 0:8], tsv[0:w, m, 0:8], s))
                    link(nc.vector.match_replace(s, tsv[0:w, m, 0:8], s, LOW))
                    link(nc.vector.max(tsv[0:w, m, 8:16], s))
                    link(nc.vector.max_index(tsi[0:w, m, 8:16], tsv[0:w, m, 8:16], s))
                v4 = tsv[0:w].rearrange("p (h a) k -> p h a k", a=2)
                full = [w, PH, TOPK, TOPK]
                c4 = cand[0:w].rearrange("p h (a b) -> p h a b", a=TOPK)
                link(nc.vector.tensor_tensor(c4, v4[:, :, 0, :].unsqueeze(3).broadcast_to(full),
                                             v4[:, :, 1, :].unsqueeze(2).broadcast_to(full), ALU.add))
                for h in range(PH):
                    s = cand[0:w, h, :]
                    link(nc.vector.max(bv[0:w, h, 0:8], s))
                    link(nc.vector.max_index(bi[0:w, h, 0:8], bv[0:w, h, 0:8], s))
                    link(nc.vector.match_replace(s, bv[0:w, h, 0:8], s, LOW))
                    link(nc.vector.max(bv[0:w, h, 8:16], s))
                    link(nc.vector.max_index(bi[0:w, h, 8:16], bv[0:w, h, 8:16], s))
                g3 = gate[0:w, t, :].rearrange("p (h k) -> p h k", h=PH)
                nc.vector.tensor_tensor(g3, bv[0:w], bv[0:w, :, 0:1].broadcast_to([w, PH, TOPK]),
                                        ALU.subtract).then_inc(s_top, 1)
                link(nc.vector.tensor_single_scalar(bu[0:w, 0], bi[0:w], 4, ALU.logical_shift_right))
                link(nc.vector.tensor_single_scalar(bu[0:w, 1], bi[0:w], 15, ALU.bitwise_and))
                link(nc.vector.tensor_copy(bt[0:w, 0:2], bu[0:w]))
                tf = hu[:, :]
                keyf = scr[0:w, 4096:4352].rearrange("p (h a k) -> p h a k", h=PH, a=2)
                link(nc.vector.tensor_copy(keyf, tsi[0:w].rearrange("p (h a) k -> p h a k", a=2)))
                iota = cols[0:w, COLS["iota"]:COLS["iota"] + TOPK].unsqueeze(1).unsqueeze(1).broadcast_to(full)
                for a in range(2):
                    link(nc.vector.tensor_tensor(oneh[0:w], bt[0:w, a].unsqueeze(3).broadcast_to(full), iota,
                                                 ALU.is_equal))
                    link(nc.vector.tensor_tensor(oneh[0:w], oneh[0:w], keyf[:, :, a, :].unsqueeze(2).broadcast_to(full),
                                                 ALU.mult))
                    link(nc.vector.tensor_reduce(bt[0:w, 2 + a], oneh[0:w], AX_X, ALU.add))
                link(nc.vector.scalar_tensor_tensor(out=idxf[0:w].rearrange("p (h k) -> p h k", h=PH), in0=bt[0:w, 2],
                                                    scalar=float(NKEY), in1=bt[0:w, 3], op0=ALU.mult, op1=ALU.add))
                link(nc.vector.tensor_copy(idx[0:w, t, :], idxf[0:w, :]))
                dve.wait_ge(s_ex, 9 + t + 1)
                link(nc.vector.tensor_reduce(st[0:w, 6, :], g3, AX_X, ALU.add))
                link(nc.vector.reciprocal(st[0:w, 7, :], st[0:w, 6, :]))
                nc.vector.tensor_tensor(g3, g3, st[0:w, 7, :].unsqueeze(2).broadcast_to([w, PH, TOPK]),
                                        ALU.mult).then_inc(s_top, 1)
                dve.wait_ge(s_top, 2 * t + 2)
            turn = 0
            for t, (t0, w) in enumerate(TILES):
                dve.wait_ge(s_xt, t + 1)
                with dve.Fori(0, NPICK // GROUP) as i:
                    for k in range(GROUP):
                        dve.wait_ge(g_in[k], (turn + i + 1) * 16)
                        nc.vector.tensor_tensor_reduce(big[0:w, k, :], big[0:w, k, :], xtok[0:w, 0, :], 1.0, 0.0, ALU.mult,
                                                       ALU.add, hu16[0:w, k:k + 1]).then_inc(g_used, 1)
                    dve.wait_ge(g_used, (turn + i + 1) * GROUP + 1)
                    nc.vector.tensor_copy(hu[0:w, bass.ds(i * GROUP, GROUP)], hu16[0:w, :]).then_inc(s_huc, 1)
                    dve.wait_ge(s_huc, turn + i + 1)
                    dve.sem_inc(s_act, 1)
                turn += NPICK // GROUP
                dve.sem_inc(s_hu, 1)
                dve.wait_ge(s_gel, t + 1)
                link(nc.vector.tensor_tensor(hu[0:w, :], hu[0:w, :], gate[0:w, t, :], ALU.mult))
                with dve.Fori(0, NPICK // GROUP) as i:
                    nc.vector.tensor_copy(a16[0:w, :], hu[0:w, bass.ds(i * GROUP, GROUP)]).then_inc(s_huc, 1)
                    dve.wait_ge(s_huc, turn + i + 1)
                    dve.sem_inc(s_act, 1)
                    for k in range(GROUP):
                        dve.wait_ge(g_in[k], (turn + i + 1) * 16)
                        nc.vector.scalar_tensor_tensor(out=acc[0:w, :], in0=big[0:w, k, :], scalar=a16[0:w, k:k + 1],
                                                       in1=acc[0:w, :], op0=ALU.mult, op1=ALU.add).then_inc(g_used, 1)
                        dve.wait_ge(g_used, (turn + i) * GROUP + k + 2)
                        dve.sem_inc(s_act, 1)
                turn += NPICK // GROUP
                dve.sem_inc(s_y, 1)


def conv_chunks(eng, ops, chunks, gpad, spad, cacc, col, s_glu, s_pz, s_stpad, s_done, link, mid, tmp=None):
    eng.wait_ge(s_pz, 1)
    eng.wait_ge(s_stpad, 16)
    for c in chunks:
        eng.wait_ge(s_glu, 2 * c + 2)
        for j in range(TAPS):
            w = col("cw", c * TAPS + j)
            for out, src in ((cacc[:, c, 0:SEQ], gpad[:, c, j:j + SEQ]),
                             (mid(cacc[:, c, SEQ:T]), spad[:, c, :, j:j + DS])):
                if j == 0:
                    ins = ops.tensor_scalar(out, src, w, col("cb", c), ALU.mult, ALU.add)
                elif tmp is None:
                    ins = ops.scalar_tensor_tensor(out=out, in0=src, scalar=w, in1=out, op0=ALU.mult, op1=ALU.add)
                else:
                    prod = tmp[:, 0:SEQ] if len(src.shape) == 2 else mid(tmp[:, SEQ:T])
                    link(ops.tensor_scalar(prod, src, w, None, ALU.mult))
                    ins = ops.tensor_tensor(out, out, prod, ALU.add)
            if j < TAPS - 1:
                link(ins)
            else:
                ins.then_inc(s_done, 1)


_OUTS = [("y", (T, D)), ("pk", (P, WIN)), ("pv", (WIN, P)), ("pc", (P, CC, PAD)), ("sk", (P, NDB, WIN)),
         ("sv", (WIN, NDB, P)), ("sc", (P, CC, NDB, PAD))]


def kernel(**inputs):
    import numpy as np
    import concourse.bacc as bacc
    from concourse.bass_utils import run_bass_kernel_spmd

    i = {k: np.asarray(v) for k, v in inputs.items()}

    def chunked(a):
        return a.reshape(-1, P, *a.shape[1:]).swapaxes(0, 1)

    x = np.concatenate([i["x_prompt"].reshape(SEQ, D), i["x_sample"].reshape(NS, D)])
    w_in, w_out, pw, wq = i["w_in"][0], i["w_out"][0], i["conv_pw_w"][0], i["peer_wq"][0]
    feat = np.array([[(g * GQ + j) * HD + d for g in range(NKV) for d in range(HD)] for j in range(GQ)])
    blocks = [w_in[:, 512:640]] + [w_in[:, feat[j]] for j in range(GQ)] + [w_in[:, 640:768]]
    for c in range(CC):
        blocks += [w_in[:, 768 + c * P:768 + (c + 1) * P], w_in[:, 1280 + c * P:1280 + (c + 1) * P]]
    blocks = [chunked(b).reshape(P, D) for b in blocks]
    pws = [chunked(pw[:, m * P:(m + 1) * P]).reshape(P, CC * P) for m in range(CC)]
    blocks += [np.concatenate(pws[0:2], 1), np.concatenate(pws[2:4], 1)]
    w_out = np.concatenate([w_out[feat.reshape(-1)], w_out[CC * P:]])
    blocks += [chunked(w_out[:, m * P:(m + 1) * P]).reshape(P, D) for m in range(DC)]
    blocks += [chunked(wq[:, m * P:(m + 1) * P]).reshape(P, D) for m in range(NM)]
    sinks = i["attn_sinks"][0]
    vec = lambda a: chunked(a.reshape(-1)).reshape(P, -1)
    row_head = np.array([(p // 32 % 2) * GQ + p % 32 // DS for p in range(P)])
    cols = [vec(i["norm1_g"]), vec(i["norm2_g"]), vec(i["attn_out_g"][0][feat.reshape(-1)]), vec(i["conv_out_g"]),
            np.tile(i["q_norm_g"][0], 2)[:, None], np.tile(i["k_norm_g"][0], 2)[:, None], vec(i["conv_b"]),
            vec(i["conv_ln_g"]), vec(i["conv_ln_b"]), chunked(i["conv_w"][0].T).reshape(P, CC * TAPS),
            np.broadcast_to(sinks, (P, NH)), sinks[row_head][:, None],
            np.broadcast_to(np.arange(TOPK, dtype=np.float32), (P, TOPK))]
    q, k = np.arange(P)[:, None], np.arange(P)[None, :]
    maskp = np.where(np.concatenate([k > q, k <= q], 1), 0.0, NEG).astype(np.float32)
    p, g, n = np.arange(P)[:, None, None], np.arange(4)[None, :, None], np.arange(NS)[None, None, :]
    s, b = p % DS, 2 * g + p // 64
    new = (n // DS == b) & (n % DS <= s)
    old = np.broadcast_to(np.arange(WIN)[None, None, :] > s, (P, 4, WIN))
    masks = np.where(np.concatenate([old, new], 2), 0.0, NEG).astype(np.float32)
    ck = i["cache_k"][0].reshape(NDB, WIN, P)
    cv = i["cache_v"][0].reshape(NDB, WIN, P)
    state = i["state_conv"][0].transpose(2, 0, 1)
    arrays = {
        "xT": chunked(x.T), "wblk": np.stack(blocks), "cols": np.concatenate(cols, 1), "maskp": maskp, "masks": masks,
        "ident": np.eye(P, dtype=np.float32), "ckT": ck.transpose(2, 0, 1), "cv": cv.transpose(1, 0, 2),
        "state": chunked(state), "keysT": i["peer_keys"][0].reshape(NM, NKEY, P).transpose(2, 0, 1),
        "u": i["peer_u"][0], "v": i["peer_v"][0],
    }
    nc = bacc.Bacc("TRN2", target_bir_lowering=False, num_devices=1)
    arrays = {k: np.ascontiguousarray(a) for k, a in arrays.items()}
    args = [nc.dram_tensor(f"in_{k}", a.shape, mybir.dt.from_np(a.dtype), kind="ExternalInput").ap()
            for k, a in arrays.items()]
    args += [nc.dram_tensor(f"out_{k}", s, F32, kind="ExternalOutput").ap() for k, s in _OUTS]
    hymba_peer(nc, *args)
    r = run_bass_kernel_spmd(nc, [{f"in_{k}": a for k, a in arrays.items()}], core_ids=[0]).results[0]
    y, pk, pv, pc, sk, sv, sc = (r[f"out_{k}"] for k, _ in _OUTS)
    return (y[:SEQ].reshape(1, SEQ, D), y[SEQ:].reshape(NDB, DS, D),
            pk.T.reshape(1, 1, WIN, NKV, HD), pv.reshape(1, 1, WIN, NKV, HD),
            pc.swapaxes(0, 1).reshape(CC * P, PAD).T.reshape(1, 1, PAD, CC * P),
            sk.transpose(1, 2, 0).reshape(1, NDB, WIN, NKV, HD), sv.transpose(1, 0, 2).reshape(1, NDB, WIN, NKV, HD),
            sc.transpose(2, 3, 1, 0).reshape(1, NDB, PAD, CC * P))
```
